# Optimizing a Trainium2 kernel written in Bass

```python
import jax, jax.numpy as jnp
from jax import lax
import numpy as np

D_MODEL = 1024
BATCH = 1
SEQ = 256
DEPTH = 2

CHUNK = 64
HEAD_DIM = 64
SB_HEADS = 8
CA_HEADS = 8
LEFT_CHUNKS = 8
REL_CLIP = 256
QBLOCK = 128
SB_W = SB_HEADS * HEAD_DIM
CA_W = CA_HEADS * HEAD_DIM
MIX_WIDTH = SB_W + CA_W
ML_HEADS = 4
ML_QK_DIM = 128
ML_V_DIM = D_MODEL // ML_HEADS
ML_QK_W = ML_HEADS * ML_QK_DIM
ML_V_W = ML_HEADS * ML_V_DIM
ML_IN_W = 2 * ML_QK_W + 2 * ML_V_W + 2 * ML_HEADS
CONV_K = 4
GATE_SOFTCAP = 15.0
D_FF = 2816
N_EXPERTS = 8
TOP_K = 2
D_FF_EXPERT = 3584
N_EVEN = (DEPTH + 1) // 2
N_ODD = DEPTH // 2
EPS = 1e-6

kernel_name = "chunk_causal_hybrid_sb_band_mlstm_moe"

def rmsnorm(x, g):
    xf = x.astype(jnp.float32)
    y = xf * lax.rsqrt(jnp.mean(xf * xf, axis=-1, keepdims=True) + EPS)
    return (y * g.astype(jnp.float32)).astype(x.dtype)

def split_heads(t, n_heads):
    b, s, _ = t.shape
    return t.reshape(b, s, n_heads, -1).transpose(0, 2, 1, 3)

def swiglu(x, wg, wu, wd):
    return (jax.nn.silu(x @ wg) * (x @ wu)) @ wd

def stick_breaking_attention(q, k, v):
    seq, d = q.shape[2], q.shape[3]
    scale = d ** -0.5
    outs = []
    for blk in range(seq // QBLOCK):
        q0 = blk * QBLOCK
        kend = q0 + QBLOCK
        qb = q[:, :, q0:kend].astype(jnp.float32)
        kb = k[:, :, :kend].astype(jnp.float32)
        vb = v[:, :, :kend].astype(jnp.float32)
        z = jnp.einsum('bhqd,bhkd->bhqk', qb, kb) * scale
        t_pos = q0 + jnp.arange(QBLOCK)[:, None]
        s_pos = jnp.arange(kend)[None, :]
        valid = s_pos < t_pos
        log_1mb = jnp.where(valid, jax.nn.log_sigmoid(-z), 0.0)
        between = lax.cumsum(log_1mb, axis=3, reverse=True) - log_1mb
        w = jnp.where(valid, jnp.exp(jax.nn.log_sigmoid(z) + between), 0.0)
        outs.append(jnp.einsum('bhqk,bhkd->bhqd', w, vb))
    return jnp.concatenate(outs, axis=2).astype(v.dtype)

def chunked_band_attention(q, k, v, rel_bias):
    b, h, seq, d = q.shape
    n_chunks = seq // CHUNK
    pad = LEFT_CHUNKS * CHUNK
    band = (LEFT_CHUNKS + 1) * CHUNK
    kp = jnp.pad(k, ((0, 0), (0, 0), (pad, 0), (0, 0)))
    vp = jnp.pad(v, ((0, 0), (0, 0), (pad, 0), (0, 0)))
    tq = jnp.arange(CHUNK)[:, None]
    jk = jnp.arange(band)[None, :]
    rel = tq + pad - jk
    bias = rel_bias[:, jnp.clip(rel, -REL_CLIP, REL_CLIP) + REL_CLIP].astype(jnp.float32)
    scale = d ** -0.5

    def one_chunk(c):
        qc = lax.dynamic_slice_in_dim(q, c * CHUNK, CHUNK, axis=2).astype(jnp.float32)
        kc = lax.dynamic_slice_in_dim(kp, c * CHUNK, band, axis=2).astype(jnp.float32)
        vc = lax.dynamic_slice_in_dim(vp, c * CHUNK, band, axis=2).astype(jnp.float32)
        s = jnp.einsum('bhqd,bhkd->bhqk', qc, kc) * scale + bias
        valid = jk >= pad - c * CHUNK
        p = jax.nn.softmax(jnp.where(valid, s, -jnp.inf), axis=-1)
        return jnp.einsum('bhqk,bhkd->bhqd', p, vc)

    out = lax.map(one_chunk, jnp.arange(n_chunks))
    return out.transpose(1, 2, 0, 3, 4).reshape(b, h, seq, d).astype(v.dtype)

def even_mixer(xn, w_in, rel_bias, w_out):
    b, s, _ = xn.shape
    u = xn @ w_in
    qa, ka, va, qb, kb, vb = jnp.split(
        u, [SB_W, 2 * SB_W, 3 * SB_W, 3 * SB_W + CA_W, 3 * SB_W + 2 * CA_W], axis=-1)
    oa = stick_breaking_attention(split_heads(qa, SB_HEADS), split_heads(ka, SB_HEADS),
                                  split_heads(va, SB_HEADS))
    ob = chunked_band_attention(split_heads(qb, CA_HEADS), split_heads(kb, CA_HEADS),
                                split_heads(vb, CA_HEADS), rel_bias)
    o = jnp.concatenate([oa, ob], axis=1)
    o = o.transpose(0, 2, 1, 3).reshape(b, s, MIX_WIDTH)
    return o @ w_out

def causal_depthwise_conv(x, w, bias):
    c = x.shape[-1]
    y = lax.conv_general_dilated(
        x, w.reshape(CONV_K, 1, c), window_strides=(1,), padding=[(CONV_K - 1, 0)],
        dimension_numbers=('NWC', 'WIO', 'NWC'), feature_group_count=c)
    return y + bias

def mlstm_chunk_step(carry, inp):
    c_mat, n_vec, m_prev = carry
    q, k, v, log_i, log_f = inp
    L = q.shape[2]
    causal = jnp.arange(L)[:, None] >= jnp.arange(L)[None, :]
    bcum = jnp.cumsum(log_f, axis=-1)
    dmat = jnp.where(causal, bcum[..., :, None] - bcum[..., None, :] + log_i[..., None, :], -jnp.inf)
    inter = bcum + m_prev[..., None]
    m_t = jnp.maximum(inter, jnp.max(dmat, axis=-1))
    scores = jnp.einsum('bhtd,bhsd->bhts', q, k) * jnp.exp(dmat - m_t[..., None])
    inter_scale = jnp.exp(inter - m_t)
    num = (jnp.einsum('bhts,bhsv->bhtv', scores, v)
           + inter_scale[..., None] * jnp.einsum('bhtd,bhdv->bhtv', q, c_mat))
    den = jnp.sum(scores, axis=-1) + inter_scale * jnp.einsum('bhtd,bhd->bht', q, n_vec)
    h = num / jnp.maximum(jnp.abs(den), jnp.exp(-m_t))[..., None]
    g = bcum[..., -1]
    decay_s = g[..., None] - bcum + log_i
    m_new = jnp.maximum(g + m_prev, jnp.max(decay_s, axis=-1))
    ws = jnp.exp(decay_s - m_new[..., None])
    carry_scale = jnp.exp(g + m_prev - m_new)
    c_new = carry_scale[..., None, None] * c_mat + jnp.einsum('bhs,bhsd,bhsv->bhdv', ws, k, v)
    n_new = carry_scale[..., None] * n_vec + jnp.einsum('bhs,bhsd->bhd', ws, k)
    return (c_new, n_new, m_new), h

def mlstm_mixer(xn, w_in, conv_w, conv_b, b_i, b_f, mh_g, w_out):
    b, s, _ = xn.shape
    n_chunks = s // CHUNK
    u = xn @ w_in
    qk, v, o_pre, gates = jnp.split(u, [2 * ML_QK_W, 2 * ML_QK_W + ML_V_W, 2 * ML_QK_W + 2 * ML_V_W], axis=-1)
    qk = jax.nn.silu(causal_depthwise_conv(qk, conv_w, conv_b))
    q, k = jnp.split(qk.astype(jnp.float32), 2, axis=-1)
    k = k * (ML_QK_DIM ** -0.5)
    gf = gates.astype(jnp.float32)
    i_pre = GATE_SOFTCAP * jnp.tanh((gf[..., :ML_HEADS] + b_i) / GATE_SOFTCAP)
    f_pre = GATE_SOFTCAP * jnp.tanh((gf[..., ML_HEADS:] + b_f) / GATE_SOFTCAP)
    log_i = i_pre
    log_f = jax.nn.log_sigmoid(f_pre)

    def to_chunks(t):
        return t.reshape(b, n_chunks, CHUNK, ML_HEADS, -1).transpose(1, 0, 3, 2, 4)

    def gate_chunks(t):
        return t.reshape(b, n_chunks, CHUNK, ML_HEADS).transpose(1, 0, 3, 2)

    xs = (to_chunks(q.reshape(b, s, ML_HEADS, ML_QK_DIM)),
          to_chunks(k.reshape(b, s, ML_HEADS, ML_QK_DIM)),
          to_chunks(v.astype(jnp.float32).reshape(b, s, ML_HEADS, ML_V_DIM)),
          gate_chunks(log_i), gate_chunks(log_f))
    init = (jnp.zeros((b, ML_HEADS, ML_QK_DIM, ML_V_DIM), jnp.float32),
            jnp.zeros((b, ML_HEADS, ML_QK_DIM), jnp.float32),
            jnp.zeros((b, ML_HEADS), jnp.float32))
    _, h = lax.scan(mlstm_chunk_step, init, xs)
    h = h.transpose(1, 0, 3, 2, 4).reshape(b, s, ML_HEADS, ML_V_DIM)
    h = h * lax.rsqrt(jnp.mean(h * h, axis=-1, keepdims=True) + EPS)
    h = h * mh_g.astype(jnp.float32).reshape(ML_HEADS, ML_V_DIM)
    h = (jax.nn.sigmoid(o_pre.astype(jnp.float32)) * h.reshape(b, s, ML_V_W)).astype(xn.dtype)
    return h @ w_out

def moe_swiglu(xn, w_router, wg, wu, wd):
    b, s, d = xn.shape
    xt = xn.reshape(b * s, d)
    logits = (xt @ w_router).astype(jnp.float32)
    top_val, top_idx = lax.top_k(logits, TOP_K)
    top_w = jax.nn.softmax(top_val, axis=-1)
    gate = jnp.sum(jax.nn.one_hot(top_idx, N_EXPERTS, dtype=jnp.float32) * top_w[..., None], axis=1)
    y = jnp.zeros_like(xt)
    for e in range(N_EXPERTS):
        y = y + gate[:, e:e + 1].astype(xt.dtype) * swiglu(xt, wg[e], wu[e], wd[e])
    return y.reshape(b, s, d)

def setup_inputs(seed: int = 0) -> dict:
    key = jax.random.key(seed)
    ks = jax.random.split(key, 24)
    f32 = jnp.float32

    def nrm(k, shape, fan_in):
        return jax.random.normal(k, shape, f32) * (fan_in ** -0.5)

    def gain(k, shape):
        return 1.0 + 0.02 * jax.random.normal(k, shape, f32)

    return {
        "x": jax.random.normal(ks[0], (BATCH, SEQ, D_MODEL), f32),
        "mix_norm_even": gain(ks[1], (N_EVEN, D_MODEL)),
        "w_in_attn": nrm(ks[2], (N_EVEN, D_MODEL, 3 * MIX_WIDTH), D_MODEL),
        "rel_bias": 0.2 * jax.random.normal(ks[3], (N_EVEN, CA_HEADS, 2 * REL_CLIP + 1), f32),
        "w_out_attn": nrm(ks[4], (N_EVEN, MIX_WIDTH, D_MODEL), MIX_WIDTH),
        "ffn_norm_even": gain(ks[5], (N_EVEN, D_MODEL)),
        "w_dense_gate": nrm(ks[6], (N_EVEN, D_MODEL, D_FF), D_MODEL),
        "w_dense_up": nrm(ks[7], (N_EVEN, D_MODEL, D_FF), D_MODEL),
        "w_dense_down": nrm(ks[8], (N_EVEN, D_FF, D_MODEL), D_FF),
        "mix_norm_odd": gain(ks[9], (N_ODD, D_MODEL)),
        "w_in_mlstm": nrm(ks[10], (N_ODD, D_MODEL, ML_IN_W), D_MODEL),
        "conv_w": nrm(ks[11], (N_ODD, CONV_K, 2 * ML_QK_W), CONV_K),
        "conv_b": 0.02 * jax.random.normal(ks[12], (N_ODD, 2 * ML_QK_W), f32),
        "b_igate": 0.1 * jax.random.normal(ks[13], (N_ODD, ML_HEADS), f32),
        "b_fgate": jnp.linspace(3.0, 6.0, ML_HEADS, dtype=f32)[None, :]
                   + 0.1 * jax.random.normal(ks[14], (N_ODD, ML_HEADS), f32),
        "mh_norm_g": gain(ks[15], (N_ODD, ML_V_W)),
        "w_out_mlstm": nrm(ks[16], (N_ODD, ML_V_W, D_MODEL), ML_V_W),
        "ffn_norm_odd": gain(ks[17], (N_ODD, D_MODEL)),
        "w_router": nrm(ks[18], (N_ODD, D_MODEL, N_EXPERTS), D_MODEL),
        "w_exp_gate": nrm(ks[19], (N_ODD, N_EXPERTS, D_MODEL, D_FF_EXPERT), D_MODEL),
        "w_exp_up": nrm(ks[20], (N_ODD, N_EXPERTS, D_MODEL, D_FF_EXPERT), D_MODEL),
        "w_exp_down": nrm(ks[21], (N_ODD, N_EXPERTS, D_FF_EXPERT, D_MODEL), D_FF_EXPERT),
        "final_norm_g": gain(ks[22], (D_MODEL,)),
    }

def reference(x, mix_norm_even, w_in_attn, rel_bias, w_out_attn, ffn_norm_even,
              w_dense_gate, w_dense_up, w_dense_down, mix_norm_odd, w_in_mlstm,
              conv_w, conv_b, b_igate, b_fgate, mh_norm_g, w_out_mlstm, ffn_norm_odd,
              w_router, w_exp_gate, w_exp_up, w_exp_down, final_norm_g):
    h = x
    for layer in range(DEPTH):
        j = layer // 2
        if layer % 2 == 0:
            h = h + even_mixer(rmsnorm(h, mix_norm_even[j]), w_in_attn[j], rel_bias[j], w_out_attn[j])
            h = h + swiglu(rmsnorm(h, ffn_norm_even[j]), w_dense_gate[j], w_dense_up[j], w_dense_down[j])
        else:
            h = h + mlstm_mixer(rmsnorm(h, mix_norm_odd[j]), w_in_mlstm[j], conv_w[j], conv_b[j],
                                b_igate[j], b_fgate[j], mh_norm_g[j], w_out_mlstm[j])
            h = h + moe_swiglu(rmsnorm(h, ffn_norm_odd[j]), w_router[j], w_exp_gate[j],
                               w_exp_up[j], w_exp_down[j])
    return rmsnorm(h, final_norm_g)


_drawn_inputs = setup_inputs


def setup_inputs(seed=0):
    import zlib

    import numpy as np

    out = dict(_drawn_inputs(seed))
    spreads = {}
    factors = {'b_igate': 64.0, 'mh_norm_g': 4.001, 'final_norm_g': 7.978, 'ffn_norm_odd': 2.748}
    for name, (base, spread) in spreads.items():
        noise = np.random.default_rng([zlib.crc32(name.encode()), seed]).standard_normal(out[name].shape)
        drawn = base * np.exp(spread * noise) if base else spread * noise
        out[name] = __import__('jax').numpy.asarray(drawn.astype(out[name].dtype))
    for name, factor in factors.items():
        out[name] = (out[name] * factor).astype(out[name].dtype)
    return out
```

```python
from contextlib import ExitStack

import concourse.bass as bass
from concourse import mybir

ALU = mybir.AluOpType
ACT = mybir.ActivationFunctionType
AX = mybir.AxisListType
F32 = mybir.dt.float32
F32R = mybir.dt.float32r
BF16 = mybir.dt.bfloat16
I32 = mybir.dt.int32
U32 = mybir.dt.uint32

P = 128
T = 256
TT = T // P
D = 1024
KT = D // P
HD = 64
NPAIR = 4
CHUNK = 64
FF = 2816
FB = 256
NFB = FF // FB
MLH = 4
MLV = 256
REL = 256
NE = 8
FE = 3584
EB = 512
NEB = FE // EB
EPS = 1e-6
NEG = -1e30
CAP = 15.0
FAR = 1000.0

W = 2048
NRAW = 6
NSPL = 3
C_OUT = 12
C_FFN = C_OUT + 4
C_MLIN = C_FFN + 3 * NFB
C_MLOUT = C_MLIN + 12
C_EXP = C_MLOUT + 4
PER_EXP = 6 * NEB
assert PER_EXP % NRAW == 0 and NRAW % NSPL == 0

V_MIXE, V_FFNE, V_MIXO, V_FFNO, V_MH, V_CB, V_CW = 0, 8, 16, 24, 32, 40, 48
NVEC = 80


def raw_slot(c):
    return c % NRAW


def split_slot(c):
    return c % NSPL


def trunk(nc, x, mix_norm_even, w_in_attn, rel_bias, w_out_attn, ffn_norm_even, w_dense_gate,
          w_dense_up, w_dense_down, mix_norm_odd, w_in_mlstm, conv_w, conv_b, b_igate, b_fgate,
          mh_norm_g, w_out_mlstm, ffn_norm_odd, w_router, w_exp_gate, w_exp_up, w_exp_down,
          final_norm_g, out):
    with ExitStack() as ctx:
        def sb(name, shape, dt=F32):
            return ctx.enter_context(nc.sbuf_tensor(name, shape, dt))

        def sem(name):
            return ctx.enter_context(nc.semaphore(name))

        raw = sb("raw", [P, NRAW, W])
        w_hi = sb("w_hi", [P, NSPL, W], F32R)
        w_lo = sb("w_lo", [P, NSPL, W], F32R)
        h = sb("h", [P, TT, D])
        xn = sb("xn", [P, TT, D])
        xt_hi = sb("xt_hi", [P, KT, T], F32R)
        xt_lo = sb("xt_lo", [P, KT, T], F32R)
        gained = sb("gained", [P, 2, 512])
        qk = sb("qk", [P, 16, T])
        vrow = sb("vrow", [P, TT, MLH, 258])
        area_a = sb("area_a", [P, 3 * 2 * 384])
        area_b = sb("area_b", [P, 8 * 384])
        area_c = sb("area_c", [P, 2 * 384])
        work = area_a[:, :].rearrange("p (s a c) -> p s a c", s=3, a=2)
        work2 = sb("work2", [P, 2, 2, 384])
        bias_t = area_b[:, :].rearrange("p (g c) -> p g c", g=8)
        probs_t = area_c[:, :].rearrange("p (a c) -> p a c", a=2)
        junk = area_a[:, 0:TT * D].rearrange("p (i d) -> p i d", i=TT)
        vecs = sb("vecs", [NVEC, P])
        vec_t = sb("vec_t", [P, NVEC])
        ident = sb("ident", [P, P])
        neg_tri = sb("neg_tri", [P, P])
        neg_one = sb("neg_one", [P, P])
        before = sb("before", [P, P])
        ones = sb("ones", [P, P])
        causal = sb("causal", [P, P])
        head_sel = sb("head_sel", [MLH, MLH, P])
        slot_no = sb("slot_no", [P, P])
        eps_c = sb("eps_c", [P, 1])
        unused = sb("unused", [P, 5])
        final_g = qk[:, 0:4, :].rearrange("p a t -> p (a t)")
        zero_b = sb("zero_b", [1, 512], BF16)
        gate_w = sb("gate_w", [P, KT, 8])
        router_w = sb("router_w", [P, KT, 8])
        narrow_hi = sb("narrow_hi", [P, KT, 8], F32R)
        narrow_lo = sb("narrow_lo", [P, KT, 8], F32R)
        gate_b = sb("gate_b", [P, 8])
        sumsq = sb("sumsq", [P, 5, TT])
        root = sb("root", [P, 5, TT])
        rstd = sb("rstd", [P, 5, TT])
        peak = sb("peak", [P, 2, 4])
        npeak = sb("npeak", [P, 2, 4])
        psum_exp = sb("psum_exp", [P, 2, 4])
        rsum = sb("rsum", [P, 2, 4])
        gates = sb("gates", [P, TT, 8])
        one_row = sb("one_row", [MLH, T])
        rows_i, rows_f, rows_a = (area_c[0:MLH, T * n:T * n + T] for n in range(3))
        rows_m, rows_x = (area_b[0:MLH, TT * D + T * n:TT * D + T * n + T] for n in range(2))
        narrow_row = area_c[0:8, 0:T]
        cols_a = sb("cols_a", [P, 2, TT, MLH])
        den = sb("den", [P, 8])
        rden = sb("rden", [P, 8])
        head_ss = sb("head_ss", [P, 8])
        head_root = sb("head_root", [P, 8])
        head_rs = sb("head_rs", [P, 8])
        logit = sb("logit", [P, TT, 8])
        top8 = sb("top8", [P, TT, 8])
        top8_i = sb("top8_i", [P, TT, 8], U32)
        top2_f = sb("top2_f", [P, TT, 2])
        ntop = sb("ntop", [P, TT])
        pair_e = sb("pair_e", [P, TT])
        pair_d = sb("pair_d", [P, TT])
        pair_w1 = sb("pair_w1", [P, TT])
        pair_w2 = sb("pair_w2", [P, TT])
        chosen1 = sb("chosen1", [P, TT, 8])
        chosen2 = sb("chosen2", [P, TT, 8])
        chosen = sb("chosen", [P, TT, 8])
        share1 = sb("share1", [P, TT, 8])
        share = sb("share", [P, TT, 9])
        slot_of = sb("slot_of", [P, TT, 9])
        slot_of2 = sb("slot_of2", [P, TT, 9])
        over = sb("over", [P, 8])
        over_key = sb("over_key", [P, 8])
        over_top = sb("over_top", [P, 8])
        over_tab = sb("over_tab", [P, 4])
        over_i = sb("over_i", [P, 4], I32)
        pick, pick_w, spread = (area_c[:, T * n:T * n + T].rearrange("p (i s) -> p i s", i=TT) for n in range(3))
        g_act = area_a[:, 0:EB]
        h_row = area_a[:, EB:2 * EB]
        y_seg = area_a[:, 2 * EB:2 * EB + D]

        ps = ctx.enter_context(nc.psum_tensor("ps", [P, 8, 512], F32))

        slots_hi, slots_lo = xt_hi[:, :, 0:P], xt_lo[:, :, 0:P]
        v_attn = vrow[:, :, :, :].rearrange("p i h c -> p (i h c)")[:, 0:2 * TT * 512].rearrange(
            "p (g i c) -> p g i c", g=2, i=TT)
        ffn_hi = sb("ffn_hi", [P, 2, 2, T], F32R)
        ffn_lo = sb("ffn_lo", [P, 2, 2, T], F32R)
        exp_hi = ffn_hi[:, 0, :, :].rearrange("p m (b t) -> p (m b) t", b=2)
        exp_lo = ffn_lo[:, 0, :, :].rearrange("p m (b t) -> p (m b) t", b=2)
        dense_s = area_a[:, 0:512].rearrange("p (m t) -> p m t", m=2)
        dense_h = area_a[:, 512:1024].rearrange("p (m t) -> p m t", m=2)
        padded = qk[:, 0:9, :].rearrange("p a t -> p (a t)")[:, 0:8 * 259].rearrange("p (a t) -> p a t", a=8)
        conv_o = area_a[:, 0:8 * T].rearrange("p (a t) -> p a t", a=8)
        osig = area_b[:, 0:TT * D].rearrange("p (i d) -> p i d", i=TT)

        raw_full = [sem(f"raw_full{i}") for i in range(NRAW)]
        hi_made, lo_made, used = sem("hi_made"), sem("lo_made"), sem("used")
        x_in, vec_in, small_in, bias_in, out_done = (sem(n) for n in (
            "x_in", "vec_in", "small_in", "bias_in", "out_done"))
        pool_step, consts, bias_ok, vec_tr, vec_ok, dve_const = (sem(n) for n in (
            "pool_step", "consts", "bias_ok", "vec_tr", "vec_ok", "dve_const"))
        squared, rooted, xn_ok, turned, gain_ok, ghi_ok, glo_ok = (sem(n) for n in (
            "squared", "rooted", "xn_ok", "turned", "gain_ok", "ghi_ok", "glo_ok"))
        nhi_ok, nlo_ok = sem("nhi_ok"), sem("nlo_ok")
        nrow_mm, nrow_ok = sem("nrow_mm"), sem("nrow_ok")
        h_ok = sem("h_ok")
        act_step, dve_step = sem("act_step"), sem("dve_step")
        q_out, kv_out = sem("q_out"), sem("kv_out")
        final_in = sem("final_in")
        z_done, b_done, o_done = sem("z_done"), sem("b_done"), sem("o_done")
        logs_ok, sp_ok, spm_ok, wexp_ok, w_ok = (sem(n) for n in ("logs_ok", "sp_ok", "spm_ok", "wexp_ok", "w_ok"))
        sc_ok, pexp_ok, p_ok, pt_ok, ohi_ok, olo_ok = (sem(n) for n in (
            "sc_ok", "pexp_ok", "p_ok", "pt_ok", "ohi_ok", "olo_ok"))
        d_silu, d_h, d_hi, d_lo = (sem(n) for n in ("d_silu", "d_h", "d_hi", "d_lo"))
        mevac_a, mevac_v, conv_ok, qk_ok, osig_ok = (sem(n) for n in (
            "mevac_a", "mevac_v", "conv_ok", "qk_ok", "osig_ok"))
        gate_mm, gate_d, gate_a, gate_pe = (sem(n) for n in ("gate_mm", "gate_d", "gate_a", "gate_pe"))
        s_mm, e_ok, pt2_ok, num_mm, hrow_ok, hss_ok, hroot_ok, hg_ok = (sem(n) for n in (
            "s_mm", "e_ok", "pt2_ok", "num_mm", "hrow_ok", "hss_ok", "hroot_ok", "hg_ok"))
        r_mm, r_d, r_a, rank_mm, table_ok = (sem(n) for n in ("r_mm", "r_d", "r_a", "rank_mm", "table_ok"))
        pick_ok, gathered, pickw_ok, pickw_tr, spread_ok = (sem(n) for n in (
            "pick_ok", "gathered", "pickw_ok", "pickw_tr", "spread_ok"))
        e_silu, e_h, e_tr, e_hi, e_lo, y_out, comb_mm, comb_add = (sem(n) for n in (
            "e_silu", "e_h", "e_tr", "e_hi", "e_lo", "y_out", "comb_mm", "comb_add"))
        fin_ok = sem("fin_ok")

        block = ctx.enter_context(nc.Block())

        G_EXP = 20

        def up_pos(n):
            return C_FFN + 1 if n == 0 else C_FFN + 3 * n

        def down_pos(n):
            return C_FFN + 4 + 3 * n if n < NFB - 1 else C_MLIN - 1

        def chunk_no(r, e=0, it=0):
            return C_EXP + r + e * PER_EXP + it * 6

        def raw_round(r, e=0, it=0):
            c = C_EXP + r
            return (c // NRAW + 1) * 16 + e * (PER_EXP // NRAW * 16) + it * 16

        FIRST = 4
        LAST = PER_EXP - 2

        @block.sync
        def _(sp):
            def load(c, src, shape):
                if c >= NRAW:
                    sp.wait_ge(lo_made, c - NRAW + 1)
                dst = raw[:, raw_slot(c), :].rearrange("p (a n) -> p a n", a=shape)
                sp.dma_start(dst, src).then_inc(raw_full[raw_slot(c)], 16)

            def rows(w, k0, k1, c0, c1):
                return w.rearrange("o (k p) n -> p (o k) n", p=P)[:, k0:k1, c0:c1]

            sp.dma_start(h[:, :, :], x.rearrange("o (i p) d -> p (o i) d", p=P)).then_inc(x_in, 16)
            for v, src in ((V_MH, mh_norm_g), (V_CB, conv_b)):
                sp.dma_start(vecs[v:v + 8, :], src.rearrange("o (k p) -> (o k) p", p=P)).then_inc(vec_in, 16)
            sp.dma_start(vecs[V_CW:V_CW + 32, :], conv_w.rearrange("o c (k p) -> (o c k) p", p=P)).then_inc(vec_in, 16)
            for b in range(6):
                for a in range(2):
                    load(2 * b + a, rows(w_in_attn, 4 * a, 4 * a + 4, 512 * b, 512 * b + 512), 4)
                if b == 1:
                    sp.dma_start(bias_t[:, :, 0:P], bass.AP(
                        tensor=rel_bias.tensor, offset=REL - (P - 1),
                        ap=[[1, P], [2 * REL + 1, 8], [1, P]])).then_inc(bias_in, 16)
                    sp.dma_start(bias_t[:, :, P:384], bass.AP(
                        tensor=rel_bias.tensor, offset=REL - (P - 1),
                        ap=[[1, P], [2 * REL + 1, 8], [1, T]])).then_inc(bias_in, 16)
            for n in range(2):
                for a in range(2):
                    load(C_OUT + 2 * n + a, rows(w_out_attn, 4 * a, 4 * a + 4, 512 * n, 512 * n + 512), 4)

            def ffn_load(c, kind, n, it=None):
                if it is None:
                    if c >= NRAW:
                        sp.wait_ge(lo_made, c - NRAW + 1)
                else:
                    sp.wait_ge(lo_made, it * 6 + (c - NRAW + 1))
                if kind == "d":
                    src = w_dense_down.rearrange("o (n k p) d -> p (o n) k d", p=P, k=2)
                    src = src[:, n, :, :] if it is None else src[:, bass.ds(n, 1), :, :].rearrange(
                        "p o k d -> p (o k) d")
                    a = 2
                else:
                    w = w_dense_gate if kind == "g" else w_dense_up
                    src = w.rearrange("o (k p) (n f) -> p (o k) n f", p=P, f=FB)
                    src = src[:, :, n, :] if it is None else src[:, :, bass.ds(n, 1), :].rearrange(
                        "p k o f -> p k (o f)")
                    a = KT
                dst = raw[:, raw_slot(c), :].rearrange("p (a n) -> p a n", a=a)
                sp.dma_start(dst, src).then_inc(raw_full[raw_slot(c)], 16)

            ffn_load(C_FFN, "g", 0)
            ffn_load(C_FFN + 1, "u", 0)
            with sp.Fori(0, (NFB - 1) // 2) as it:
                for s in range(2):
                    c = C_FFN + 2 + 3 * s
                    ffn_load(c, "g", it * 2 + (1 + s), it)
                    ffn_load(c + 1, "u", it * 2 + (1 + s), it)
                    ffn_load(c + 2, "d", it * 2 + s, it)
            ffn_load(C_MLIN - 1, "d", NFB - 1)
            for b in range(6):
                for a in range(2):
                    load(C_MLIN + 2 * b + a, rows(w_in_mlstm, 4 * a, 4 * a + 4, 512 * b, 512 * b + 512), 4)
            for n in range(2):
                for a in range(2):
                    load(C_MLOUT + 2 * n + a, rows(w_out_mlstm, 4 * a, 4 * a + 4, 512 * n, 512 * n + 512), 4)

            def expert_loads(seg, expert):
                def one(r, kind, a, j, it):
                    sp.wait_ge(lo_made, chunk_no(r, seg, it) - (NRAW - 1))
                    if kind == "d":
                        src = w_exp_down.rearrange("o e (j k p) d -> p (o e) j k d", p=P, k=4)
                        src = src[:, bass.ds(expert, 1), bass.ds(j, 1), 2 * a:2 * a + 2, :].rearrange(
                            "p e j k d -> p (e j k) d")
                        n = 2
                    else:
                        w = w_exp_gate if kind == "g" else w_exp_up
                        src = w.rearrange("o e (k p) (j f) -> p (o e) k j f", p=P, f=EB)
                        src = src[:, bass.ds(expert, 1), 4 * a:4 * a + 4, bass.ds(j, 1), :].rearrange(
                            "p e k j f -> p (e k) (j f)")
                        n = 4
                    s = raw_slot(C_EXP + r)
                    sp.dma_start(raw[:, s, :].rearrange("p (a n) -> p a n", a=n), src).then_inc(raw_full[s], 16)

                for r, (kind, a) in enumerate([("g", 0), ("g", 1), ("u", 0), ("u", 1)]):
                    one(r, kind, a, 0, 0)
                with sp.Fori(0, NEB - 1) as it:
                    for k, (kind, a) in enumerate([("g", 0), ("g", 1), ("u", 0), ("u", 1)]):
                        one(FIRST + k, kind, a, it + 1, it)
                    for a in range(2):
                        one(FIRST + 4 + a, "d", a, it, it)
                for a in range(2):
                    one(LAST + a, "d", a, NEB - 1, 0)

            with sp.Fori(0, NE) as e:
                expert_loads(e, e)
            sp.wait_ge(table_ok, 1)
            n_over = sp.value_load(over_i[0:1, 3:4], min_val=0, max_val=3)
            with sp.Fori(0, 3) as j:
                with sp.If(n_over > j):
                    expert = sp.value_load(over_i[0:1, bass.ds(j, 1)], min_val=0, max_val=NE - 1)
                    expert_loads(j + NE, expert)
            for i in range(TT):
                sp.wait_ge(fin_ok, i + 1)
                sp.dma_start(out.rearrange("o (i p) d -> p (o i) d", p=P)[:, i, :],
                             xn[:, i, :]).then_inc(out_done, 16)
            sp.wait_ge(out_done, 16 * TT)

        @block.gpsimd
        def _(pool):
            n = [0]

            def done(ins):
                n[0] += 1
                ins.then_inc(pool_step, 1)
                pool.wait_ge(pool_step, n[0])

            done(pool.memset(ident[:, :], 0.0))
            done(pool.memset(neg_tri[:, :], -1.0))
            done(pool.memset(neg_one[:, :], -1.0))
            done(pool.memset(before[:, :], 1.0))
            done(pool.memset(ones[:, :], 1.0))
            done(pool.memset(causal[:, :], 0.0))
            done(pool.memset(head_sel[:, :, :], 0.0))
            done(pool.memset(eps_c[:, :], EPS))
            done(pool.memset(zero_b[:, :], 0.0))
            done(pool.memset(one_row[:, :], 1.0))
            done(pool.affine_select(out=ident[:, :], in_=ident[:, :], compare_op=ALU.not_equal, fill=1.0,
                                    base=0, pattern=[[-1, P]], channel_multiplier=1))
            done(pool.affine_select(out=neg_tri[:, :], in_=neg_tri[:, :], compare_op=ALU.is_ge, fill=0.0,
                                    base=0, pattern=[[-1, P]], channel_multiplier=1))
            done(pool.affine_select(out=before[:, :], in_=before[:, :], compare_op=ALU.is_gt, fill=0.0,
                                    base=0, pattern=[[1, P]], channel_multiplier=-1))
            done(pool.affine_select(out=causal[:, :], in_=causal[:, :], compare_op=ALU.is_ge, fill=NEG,
                                    base=0, pattern=[[1, P]], channel_multiplier=-1))
            done(pool.affine_select(out=head_sel[:, :, :], in_=head_sel[:, :, :], compare_op=ALU.not_equal,
                                    fill=1.0, base=0, pattern=[[-1, MLH], [0, P]], channel_multiplier=1))
            pool.iota(slot_no[:, :], pattern=[[1, P]], base=0, channel_multiplier=0,
                      allow_small_or_imprecise_dtypes=True).then_inc(consts, 1)
            pool.dma_start(gate_w[:, :, :], w_in_mlstm.rearrange("o (k p) n -> p (o k) n", p=P)[:, :, 3072:3080]).then_inc(small_in, 16)
            pool.dma_start(router_w[:, :, :], w_router.rearrange("o (k p) n -> p (o k) n", p=P)).then_inc(small_in, 16)
            pool.dma_start(gate_b[:, 0:4], bass.AP(tensor=b_igate.tensor, offset=0, ap=[[0, P], [1, 4]])).then_inc(small_in, 16)
            pool.dma_start(gate_b[:, 4:8], bass.AP(tensor=b_fgate.tensor, offset=0, ap=[[0, P], [1, 4]])).then_inc(small_in, 16)
            pool.wait_ge(bias_in, 32)
            done(pool.memset(bias_t[0:CHUNK, :, 0:CHUNK], NEG))
            pool.memset(bias_t[0:CHUNK, :, P:P + CHUNK], NEG).then_inc(bias_ok, 1)

            def diag(buf, s):
                for a in range(2):
                    v = buf[:, s, a, :]
                    for q in (0, T):
                        ins = pool.affine_select(out=v[:, q:q + P], in_=v[:, q:q + P], compare_op=ALU.is_gt,
                                                 fill=0.0, base=0, pattern=[[1, P]], channel_multiplier=-1)
                return ins

            for i in range(0, 2 * NPAIR + 2):
                if i < 2 * NPAIR and i % 2 == 0:
                    pool.wait_ge(sp_ok, i // 2 + 1)
                    diag(work, i // 2 % 2).then_inc(spm_ok, 1)
                if 1 <= i < 2 * NPAIR and (i - 1) % 2 == 0:
                    pool.wait_ge(wexp_ok, (i - 1) // 2 + 1)
                    diag(work2, 0).then_inc(w_ok, 1)
            pool.wait_ge(h_ok, 12)
            pool.dma_start(final_g, bass.AP(tensor=final_norm_g.tensor, offset=0,
                                            ap=[[0, P], [1, D]])).then_inc(final_in, 16)

        @block.scalar
        def _(act):
            cursor = [0]
            steps = [0]

            def hi(c):
                act.wait_ge(raw_full[raw_slot(c)], 16 * (c // NRAW + 1))
                if c >= NSPL:
                    act.wait_ge(used, c - NSPL + 1)
                act.activation(w_hi[:, split_slot(c), :], raw[:, raw_slot(c), :], ACT.Copy).then_inc(hi_made, 1)

            def hi_upto(n):
                while cursor[0] < n:
                    hi(cursor[0])
                    cursor[0] += 1

            def hi_loop(c, it):
                act.wait_ge(raw_full[raw_slot(c)], it * 16 + 16 * (c // NRAW + 1))
                act.wait_ge(used, it * 6 + (c - NSPL + 1))
                act.activation(w_hi[:, split_slot(c), :], raw[:, raw_slot(c), :], ACT.Copy).then_inc(hi_made, 1)

            def link(ins):
                steps[0] += 1
                ins.then_inc(act_step, 1)
                act.wait_ge(act_step, steps[0])

            def norm(n):
                for i in range(TT):
                    act.activation(junk[:, i, :], h[:, i, :], ACT.Square,
                                   accum_out=sumsq[:, n, i:i + 1]).then_inc(squared, 1)
                act.wait_ge(squared, TT * (n + 1))
                act.activation(root[:, n, :], sumsq[:, n, :], ACT.Sqrt, bias=eps_c[:, 0:1],
                               scale=1.0 / D).then_inc(rooted, 1)

            def set_sqrt(n):
                act.activation(unused[:, n:n + 1], eps_c[:, 0:1], ACT.Sqrt)

            def gained_hi(g, dst):
                act.wait_ge(gain_ok, g + 1)
                act.activation(dst, gained[:, g % 2, :].rearrange("p (k t) -> p k t", t=P), ACT.Copy).then_inc(ghi_ok, 1)

            def norm_hi(g0):
                for i in range(TT):
                    for b in range(2):
                        gained_hi(g0 + 2 * i + b, xt_hi[:, 4 * b:4 * b + 4, i * P:(i + 1) * P])

            for v, src in ((V_MIXE, mix_norm_even), (V_FFNE, ffn_norm_even), (V_MIXO, mix_norm_odd), (V_FFNO, ffn_norm_odd)):
                act.dma_start(vecs[v:v + 8, :], src.rearrange("o (k p) -> (o k) p", p=P)).then_inc(vec_in, 16)
            act.wait_ge(consts, 1)
            act.wait_ge(x_in, 16)
            norm(0)
            act.wait_ge(vec_tr, 1)
            act.activation(vec_t[:, :], ps[:, 7, 0:NVEC], ACT.Copy).then_inc(vec_ok, 1)
            hi_upto(2)
            norm_hi(0)
            for b in range(6):
                hi_upto(min(2 * b + 4, C_OUT))
                if b in (0, 3):
                    act.wait_ge(used, 2 * b + 2)
                    act.activation(qk[:, (0, 0, 0, 8)[b]:(0, 0, 0, 8)[b] + 4, :], ps[:, 4 * (b % 2):4 * (b % 2) + 4, 0:T],
                                   ACT.Copy, scale=HD ** -0.5).then_inc(q_out, 1)
            hi_upto(C_OUT + 3)
            for i in range(2 * NPAIR + 2):
                if i < 2 * NPAIR:
                    u, z = i // 2, 2 * (i % 2)
                    if i % 2 == 0:
                        act.wait_ge(z_done, i + 1)
                        if u >= 1:
                            act.wait_ge(sp_ok, u)
                        link(act.activation(work[:, 2, :, :], ps[:, z:z + 2, 0:384], ACT.Abs))
                        link(act.activation(work[:, 2, :, :], work[:, 2, :, :], ACT.Exp, scale=-1.0))
                        act.activation(work[:, 2, :, :], work[:, 2, :, :], ACT.Ln, bias=1.0).then_inc(logs_ok, 1)
                    else:
                        act.wait_ge(sc_ok, u + 1)
                        for a in range(2):
                            for t, (c0, c1) in enumerate(((0, P), (P, 384))):
                                k = 2 * a + t
                                ins = act.activation(work2[:, 1, a, c0:c1], work2[:, 1, a, c0:c1], ACT.Exp,
                                                     bias=npeak[:, u % 2, k:k + 1],
                                                     accum_out=psum_exp[:, u % 2, k:k + 1])
                        ins.then_inc(pexp_ok, 1)
                if 1 <= i <= 2 * NPAIR and (i - 1) % 2 == 0:
                    j = i - 1
                    act.wait_ge(b_done, j + 1)
                    if j >= 2:
                        act.wait_ge(o_done, j - 1)
                    act.activation(work2[:, 0, :, :], ps[:, 0:2, 0:384], ACT.Exp).then_inc(wexp_ok, 1)
                if i >= 2:
                    j = i - 2
                    act.wait_ge(o_done, j + 1)
                    act.activation(xt_hi[:, j // 2 + 4 * (j % 2), :], ps[:, 4 + j % 2, 0:T], ACT.Copy).then_inc(ohi_ok, 1)
            set_sqrt(1)
            hi_upto(C_FFN + 2)
            act.wait_ge(h_ok, 4)
            norm(1)
            norm_hi(4)
            hi_upto(C_FFN + 3)

            def d_step(n, it=0, up=True, down=True, nxt=True):
                if up:
                    hi_loop(C_FFN + 2 + 3 * n + 1, it)
                act.wait_ge(used, it * 6 + up_pos(n) + 1)
                if n:
                    act.wait_ge(d_h, it * 2 + n)
                act.activation(dense_s[:, :, :], ps[:, 0:2, 0:T], ACT.Silu).then_inc(d_silu, 1)
                act.wait_ge(d_h, it * 2 + n + 1)
                if n >= 2:
                    act.wait_ge(used, it * 6 + down_pos(n - 2) + 1)
                act.activation(ffn_hi[:, n % 2, :, :], dense_h[:, :, :], ACT.Copy).then_inc(d_hi, 1)
                if down:
                    hi_loop(down_pos(n), it)
                if nxt:
                    hi_loop(C_FFN + 2 + 3 * (n + 1), it)

            d_step(0)
            d_step(1)
            d_step(2)
            with act.Fori(0, 3) as it:
                d_step(3, it)
                d_step(4, it)
            d_step(9, nxt=False)
            d_step(10, up=False, nxt=False)
            cursor[0] = C_MLIN
            set_sqrt(2)
            act.wait_ge(small_in, 64)
            act.activation(narrow_hi[:, :, :], gate_w[:, :, :], ACT.Copy).then_inc(nhi_ok, 1)
            hi_upto(C_MLIN + 2)
            act.wait_ge(h_ok, 8)
            norm(2)
            norm_hi(8)
            hi_upto(C_MLIN + 3)
            act.wait_ge(gate_d, 1)
            act.activation(gates[:, :, :], gates[:, :, :], ACT.Tanh).then_inc(gate_a, 1)
            act.wait_ge(gate_a, 1)
            act.activation(gates[:, :, 4:8], gates[:, :, 4:8], ACT.Exp, scale=-CAP).then_inc(gate_a, 1)
            act.wait_ge(gate_a, 2)
            act.activation(gates[:, :, 4:8], gates[:, :, 4:8], ACT.Ln, bias=1.0).then_inc(gate_a, 1)

            for b in range(6):
                hi_upto(min(C_MLIN + 2 * b + 4, C_MLOUT))
                if b < 2:
                    act.wait_ge(used, C_MLIN + 2 * b + 2)
                    act.activation(padded[:, 4 * b:4 * b + 4, 3:259], ps[:, 4 * (b % 2):4 * (b % 2) + 4, 0:T],
                                   ACT.Copy).then_inc(mevac_a, 1)
                elif b >= 4:
                    if b == 4:
                        act.wait_ge(gate_d, 4)
                        act.activation(rows_x[:, :], rows_x[:, :], ACT.Exp).then_inc(gate_a, 1)
                    act.wait_ge(used, C_MLIN + 2 * b + 2)
                    act.activation(osig[:, :, 512 * (b - 4):512 * (b - 4) + 512], ps[:, 4 * (b % 2):4 * (b % 2) + 2, :],
                                   ACT.Sigmoid).then_inc(osig_ok, 1)
            for k in range(8):
                act.wait_ge(conv_ok, k + 1)
                act.activation(conv_o[:, k, :], conv_o[:, k, :], ACT.Silu, bias=vec_t[:, V_CB + k:V_CB + k + 1]).then_inc(qk_ok, 1)
            for g in range(MLH):
                b = 2 * (g % 2) + 1
                act.wait_ge(s_mm, g + 1)
                act.wait_ge(gate_d, 5)
                if g >= 2:
                    act.wait_ge(pt2_ok, g - 1)
                act.activation(work2[:, g % 2, 0, 0:T], ps[:, b, 0:T], ACT.Exp, bias=cols_a[:, 0, 0, g:g + 1])
                act.activation(work2[:, g % 2, 0, T:384], ps[:, b, T:384], ACT.Exp,
                               bias=cols_a[:, 0, 1, g:g + 1]).then_inc(e_ok, 1)
            hi_upto(C_MLOUT + 2)
            act.wait_ge(gate_mm, 1)
            act.wait_ge(nlo_ok, 1)
            act.activation(narrow_hi[:, :, :], router_w[:, :, :], ACT.Copy).then_inc(nhi_ok, 1)
            set_sqrt(3)
            for g in range(MLH):
                act.wait_ge(hrow_ok, 2 * g + 2)
                for i in range(TT):
                    act.activation(qk[:, 2 * g + i, :], xn[:, i, g * MLV:(g + 1) * MLV], ACT.Square,
                                   accum_out=head_ss[:, 2 * g + i:2 * g + i + 1]).then_inc(hss_ok, 1)
            act.wait_ge(hss_ok, 8)
            act.activation(head_root[:, :], head_ss[:, :], ACT.Sqrt, bias=eps_c[:, 0:1], scale=1.0 / MLV).then_inc(hroot_ok, 1)
            norm_hi(12)
            hi_upto(C_EXP)
            hi_upto(C_EXP + 2)
            act.wait_ge(h_ok, 12)
            norm(3)
            norm_hi(16)
            hi_upto(C_EXP + 3)
            act.wait_ge(r_d, 1)
            for i in range(TT):
                ins = act.activation(pair_e[:, i:i + 1], top8[:, i, 1:2], ACT.Exp, bias=ntop[:, i:i + 1])
            ins.then_inc(r_a, 1)
            act.activation(head_ss[:, 0:1], head_ss[:, 0:1], ACT.Silu)

            def seg_hi(r, seg, it=0):
                c = C_EXP + r
                act.wait_ge(raw_full[raw_slot(c)], raw_round(r, seg, it))
                act.wait_ge(used, chunk_no(r, seg, it) - (NSPL - 1))
                act.activation(w_hi[:, split_slot(c), :], raw[:, raw_slot(c), :], ACT.Copy).then_inc(hi_made, 1)

            def seg_hidden_hi(blk):
                act.wait_ge(e_tr, blk + 1)
                act.activation(exp_hi, ps[:, 2, :].rearrange("p (m t) -> p m t", m=4), ACT.Copy).then_inc(e_hi, 1)

            def seg_gather_hi(g):
                for b in range(2):
                    act.wait_ge(gain_ok, g + (b + 1))
                    act.activation(slots_hi[:, 4 * b:4 * b + 4, :], gained[:, b, :].rearrange("p (k t) -> p k t", t=P),
                                   ACT.Copy).then_inc(ghi_ok, 1)

            def segment(seg, main):
                for r in (3, FIRST, FIRST + 1):
                    seg_hi(r, seg)
                act.wait_ge(used, chunk_no(FIRST, seg))
                act.wait_ge(e_h, seg * NEB + 1)
                act.activation(g_act, ps[:, 0, :], ACT.Silu).then_inc(e_silu, 1)
                act.wait_ge(pickw_tr, seg + 1)
                act.activation(spread[:, :, :], ps[:, 7, 0:T].rearrange("p (i t) -> p i t", i=TT), ACT.Copy).then_inc(spread_ok, 1)
                with act.Fori(0, NEB - 1) as it:
                    blk = seg * NEB + it
                    seg_hi(FIRST + 2, seg, it)
                    seg_hi(FIRST + 3, seg, it)
                    seg_hidden_hi(blk)
                    seg_hi(FIRST + 4, seg, it)
                    seg_hi(FIRST + 5, seg, it)
                    act.wait_ge(used, chunk_no(FIRST + 4, seg, it))
                    act.wait_ge(e_h, blk + 2)
                    act.activation(g_act, ps[:, 0, :], ACT.Silu).then_inc(e_silu, 1)
                    seg_hi(FIRST + 6, seg, it)
                    seg_hi(FIRST + 7, seg, it)
                seg_hidden_hi(seg * NEB + (NEB - 1))
                if main:
                    with act.If(seg < NE - 1):
                        seg_hi(PER_EXP, seg)
                    seg_gather_hi(seg * 2 + (G_EXP + 2))
                    with act.If(seg < NE - 1):
                        seg_hi(PER_EXP + 1, seg)
                act.wait_ge(used, chunk_no(PER_EXP, seg))
                act.activation(y_seg.rearrange("p (a n) -> p a n", a=2), ps[:, 3:5, :], ACT.Copy).then_inc(y_out, 1)
                if main:
                    with act.If(seg < NE - 1):
                        seg_hi(PER_EXP + 2, seg)

            seg_gather_hi(G_EXP)
            with act.Fori(0, NE) as e:
                segment(e, True)
            act.wait_ge(table_ok, 1)
            n_over = act.value_load(over_i[0:1, 3:4], min_val=0, max_val=3)
            with act.Fori(0, 3) as j:
                with act.If(n_over > j):
                    seg_hi(0, j + NE)
                    seg_hi(1, j + NE)
                    seg_gather_hi(j * 2 + (G_EXP + 2 * (NE + 1)))
                    seg_hi(2, j + NE)
                    segment(j + NE, False)
            set_sqrt(4)
            act.wait_ge(h_ok, 13)
            norm(4)

        @block.vector
        def _(dve):
            cursor = [0]
            steps = [0]

            def lo_at(c):
                dve.tensor_tensor(w_lo[:, split_slot(c), :], raw[:, raw_slot(c), :],
                                  w_hi[:, split_slot(c), :].bitcast(F32), ALU.subtract).then_inc(lo_made, 1)

            def lo_upto(n):
                while cursor[0] < n:
                    dve.wait_ge(hi_made, cursor[0] + 1)
                    lo_at(cursor[0])
                    cursor[0] += 1

            def lo_loop(c, it):
                dve.wait_ge(hi_made, it * 6 + (c + 1))
                lo_at(c)

            def link(ins):
                steps[0] += 1
                ins.then_inc(dve_step, 1)
                dve.wait_ge(dve_step, steps[0])

            def norm(n):
                dve.wait_ge(rooted, n + 1)
                link(dve.reciprocal(rstd[:, n, :], root[:, n, :]))
                for i in range(TT):
                    dve.tensor_scalar(xn[:, i, :], h[:, i, :], rstd[:, n, i:i + 1], None, ALU.mult).then_inc(xn_ok, 1)

            def gain(g, v, b, bank):
                out = gained[:, g % 2, :].rearrange("p (k t) -> p k t", t=P)
                dve.wait_ge(turned, g + 1)
                dve.tensor_tensor(out, ps[:, bank, :].rearrange("p (k t) -> p k t", t=P),
                                  vec_t[:, v + 4 * b:v + 4 * b + 4].unsqueeze(2).to_broadcast([P, 4, P]),
                                  ALU.mult).then_inc(gain_ok, 1)

            def gained_lo(g, dst_lo, dst_hi):
                dve.wait_ge(ghi_ok, g + 1)
                dve.tensor_tensor(dst_lo, gained[:, g % 2, :].rearrange("p (k t) -> p k t", t=P),
                                  dst_hi.bitcast(F32), ALU.subtract).then_inc(glo_ok, 1)

            def norm_split(g0, v):
                def lo_of(q):
                    i, b = q // 2, q % 2
                    gained_lo(g0 + q, xt_lo[:, 4 * b:4 * b + 4, i * P:(i + 1) * P],
                              xt_hi[:, 4 * b:4 * b + 4, i * P:(i + 1) * P])
                gain(g0, v, 0, 0)
                gain(g0 + 1, v, 1, 1)
                lo_of(0)
                dve.wait_ge(glo_ok, g0 + 1)
                gain(g0 + 2, v, 0, 2)
                lo_of(1)
                dve.wait_ge(glo_ok, g0 + 2)
                gain(g0 + 3, v, 1, 3)
                lo_of(2)
                lo_of(3)

            def add_h(src_bank, i, n):
                dve.tensor_tensor(h[:, i, 512 * n:512 * n + 512], h[:, i, 512 * n:512 * n + 512],
                                  ps[:, src_bank, :], ALU.add).then_inc(h_ok, 1)

            dve.memset(share[:, :, 8:9], 0.0).then_inc(e_h, 1)
            dve.memset(pair_e[:, :], 0.0).then_inc(comb_add, 5)
            dve.memset(pair_d[:, :], 0.0).then_inc(comb_mm, 4)
            dve.memset(pair_w1[:, :], 0.0).then_inc(y_out, 1)
            dve.memset(pair_w2[:, :], 0.0).then_inc(spread_ok, 1)
            norm(0)
            lo_upto(1)
            dve.wait_ge(vec_ok, 1)
            norm_split(0, V_MIXE)
            for b in range(6):
                lo_upto(min(2 * b + 4, C_OUT))
                if b in (1, 4):
                    dve.wait_ge(used, 2 * b + 2)
                    d = 4 if b == 1 else 12
                    dve.tensor_copy(qk[:, d:d + 4, :], ps[:, 4 * (b % 2):4 * (b % 2) + 4, 0:T]).then_inc(kv_out, 1)
                if b in (2, 5):
                    dve.wait_ge(used, 2 * b + 2)
                    dve.tensor_copy(v_attn[:, b // 3, :, :], ps[:, 4 * (b % 2):4 * (b % 2) + 2, :]).then_inc(kv_out, 1)
            lo_upto(C_OUT + 3)
            for i in range(2 * NPAIR + 2):
                if i < 2 * NPAIR:
                    u, z = i // 2, 2 * (i % 2)
                    if i % 2 == 0:
                        dve.wait_ge(logs_ok, u + 1)
                        if u >= 2:
                            dve.wait_ge(b_done, 2 * (u - 2) + 1)
                        dve.scalar_tensor_tensor(out=work[:, u % 2, :, :], in0=ps[:, z:z + 2, 0:384], scalar=0.0,
                                                 in1=work[:, 2, :, :], op0=ALU.max, op1=ALU.add).then_inc(sp_ok, 1)
                    else:
                        dve.wait_ge(z_done, i + 1)
                        dve.wait_ge(bias_ok, 1)
                        if u >= 1:
                            dve.wait_ge(b_done, i - 1)
                        heads = bias_t[:, 2 * u:2 * u + 2, :]
                        dve.tensor_tensor(work2[:, 1, :, 0:P], ps[:, z:z + 2, 0:P], heads[:, :, 0:P][:, :, ::-1], ALU.add)
                        link(dve.tensor_tensor(work2[:, 1, :, P:384], ps[:, z:z + 2, P:384],
                                               heads[:, :, P:384][:, :, ::-1], ALU.add))
                        pk = peak[:, u % 2, :].rearrange("p (a t) -> p a t", t=2)
                        dve.tensor_reduce(pk[:, :, 0:1], work2[:, 1, :, 0:P], AX.X, ALU.max)
                        link(dve.tensor_reduce(pk[:, :, 1:2], work2[:, 1, :, P:384], AX.X, ALU.max))
                        dve.tensor_scalar(npeak[:, u % 2, :], peak[:, u % 2, :], -1.0, None, ALU.mult).then_inc(sc_ok, 1)
                        dve.wait_ge(pexp_ok, u + 1)
                        link(dve.reciprocal(rsum[:, u % 2, :], psum_exp[:, u % 2, :]))
                        for a in range(2):
                            for t, (c0, c1) in enumerate(((0, P), (P, 384))):
                                k = 2 * a + t
                                ins = dve.tensor_scalar(work2[:, 1, a, c0:c1], work2[:, 1, a, c0:c1],
                                                        rsum[:, u % 2, k:k + 1], None, ALU.mult)
                        ins.then_inc(p_ok, 1)
                if 1 <= i <= 2 * NPAIR and (i - 1) % 2 == 1:
                    j = i - 1
                    dve.wait_ge(b_done, j + 1)
                    if j >= 3:
                        dve.wait_ge(o_done, j - 1)
                    dve.tensor_copy(probs_t, ps[:, 2:4, 0:384]).then_inc(pt_ok, 1)
                if i >= 2:
                    j = i - 2
                    t = j // 2 + 4 * (j % 2)
                    dve.wait_ge(ohi_ok, j + 1)
                    dve.tensor_tensor(xt_lo[:, t, :], ps[:, 4 + j % 2, 0:T], xt_hi[:, t, :].bitcast(F32),
                                      ALU.subtract).then_inc(olo_ok, 1)
            lo_upto(C_FFN)
            for n in range(2):
                for i in range(TT):
                    dve.wait_ge(used, C_OUT + 2 * n + 2)
                    add_h(2 * n + i, i, n)
            lo_upto(C_FFN + 2)
            norm(1)
            norm_split(4, V_FFNE)
            lo_upto(C_FFN + 3)

            def d_step(n, it=0, up=True, down=True, nxt=True):
                if up:
                    lo_loop(C_FFN + 2 + 3 * n + 1, it)
                dve.wait_ge(d_silu, it * 2 + n + 1)
                if n:
                    dve.wait_ge(d_lo, it * 2 + n)
                dve.tensor_tensor(dense_h[:, :, :], dense_s[:, :, :], ps[:, 2:4, 0:T], ALU.mult).then_inc(d_h, 1)
                dve.wait_ge(d_hi, it * 2 + n + 1)
                dve.tensor_tensor(ffn_lo[:, n % 2, :, :], dense_h[:, :, :], ffn_hi[:, n % 2, :, :].bitcast(F32),
                                  ALU.subtract).then_inc(d_lo, 1)
                if down:
                    lo_loop(down_pos(n), it)
                if nxt:
                    lo_loop(C_FFN + 2 + 3 * (n + 1), it)

            d_step(0)
            d_step(1)
            d_step(2)
            with dve.Fori(0, 3) as it:
                d_step(3, it)
                d_step(4, it)
            d_step(9, nxt=False)
            d_step(10, up=False, nxt=False)
            cursor[0] = C_MLIN
            for q in range(4):
                dve.wait_ge(used, C_MLIN)
                add_h(4 + q, q // 2, q % 2)
            lo_upto(C_MLIN + 2)
            dve.wait_ge(nhi_ok, 1)
            dve.tensor_tensor(narrow_lo[:, :, :], gate_w[:, :, :], narrow_hi[:, :, :].bitcast(F32),
                              ALU.subtract).then_inc(nlo_ok, 1)
            dve.memset(padded[:, :, 0:3], 0.0).then_inc(dve_const, 1)
            dve.memset(vrow[:, :, :, MLV:MLV + 1], 1.0).then_inc(dve_const, 1)
            norm(2)
            norm_split(8, V_MIXO)
            dve.wait_ge(nrow_mm, 1)
            dve.tensor_copy(narrow_row, ps[0:8, 7, T:2 * T]).then_inc(nrow_ok, 1)
            dve.wait_ge(gate_mm, 1)
            dve.wait_ge(small_in, 64)
            for i in range(TT):
                ins = dve.tensor_tensor(gates[:, i, :], ps[:, 7, 8 * i:8 * i + 8], gate_b[:, :], ALU.add)
            link(ins)
            dve.tensor_scalar(gates[:, :, :], gates[:, :, :], 1.0 / CAP, None, ALU.mult).then_inc(gate_d, 1)
            def gate_rows():
                dve.wait_ge(gate_pe, 1)
                dve.tensor_scalar(rows_i[:, :], ps[0:MLH, 6, 0:T], CAP, None, ALU.mult).then_inc(gate_d, 1)
                dve.tensor_copy(rows_f[:, :], ps[0:MLH, 6, T:512]).then_inc(gate_d, 1)
                dve.wait_ge(gate_d, 3)
                link(dve.tensor_tensor_scan(rows_x[:, :], one_row[:, :], rows_f[:, :], 0.0, ALU.mult, ALU.add))
                link(dve.tensor_tensor(rows_a[:, :], rows_i[:, :], rows_x[:, :], ALU.add))
                link(dve.tensor_tensor_scan(rows_m[:, :], rows_a[:, :], rows_a[:, :], 0.0, ALU.max, ALU.max))
                link(dve.tensor_tensor(rows_x[:, :], rows_x[:, :], rows_m[:, :], ALU.subtract))
                dve.tensor_scalar(rows_m[:, :], rows_m[:, :], -1.0, None, ALU.mult).then_inc(gate_d, 1)

            for b in range(6):
                lo_upto(min(C_MLIN + 2 * b + 4, C_MLOUT))
                if b in (2, 3):
                    dve.wait_ge(used, C_MLIN + 2 * b + 2)
                    for i in range(TT):
                        ins = dve.tensor_copy(vrow[:, i, 2 * (b - 2):2 * (b - 2) + 2, 0:MLV],
                                              ps[:, 4 * (b % 2) + i, :].rearrange("p (a c) -> p a c", a=2))
                    ins.then_inc(mevac_v, 1)
                if b == 3:
                    gate_rows()
                if b >= 2:
                    for k in (2 * (b - 2), 2 * (b - 2) + 1):
                        dve.wait_ge(mevac_a, k // 4 + 1)
                        link(dve.tensor_scalar(conv_o[:, k, :], padded[:, k, 0:T],
                                               vec_t[:, V_CW + k:V_CW + k + 1], None, ALU.mult))
                        for tap in range(1, 4):
                            ins = dve.scalar_tensor_tensor(
                                out=conv_o[:, k, :], in0=padded[:, k, tap:tap + T],
                                scalar=vec_t[:, V_CW + 8 * tap + k:V_CW + 8 * tap + k + 1],
                                in1=conv_o[:, k, :], op0=ALU.mult, op1=ALU.add)
                            if tap < 3:
                                link(ins)
                        ins.then_inc(conv_ok, 1)
            dve.wait_ge(gate_pe, 2)
            dve.tensor_copy(cols_a[:, :, :, :].rearrange("p x i g -> p (x i g)"), ps[:, 6, 0:16]).then_inc(gate_d, 1)
            for i in range(MLH + 1):
                if i < MLH:
                    g = i
                    dve.wait_ge(e_ok, g + 1)
                    dve.scalar_tensor_tensor(out=work2[:, g % 2, 1, :], in0=ps[:, 2 * (g % 2), 0:384], scalar=P ** -0.5,
                                             in1=work2[:, g % 2, 0, :], op0=ALU.mult, op1=ALU.mult).then_inc(pt2_ok, 1)
                if i >= 1:
                    g = i - 1
                    dve.wait_ge(num_mm, g + 1)
                    dve.wait_ge(gate_d, 5)
                    for t in range(TT):
                        k = 2 * g + t
                        b = 4 + 2 * (g % 2) + t
                        link(dve.tensor_scalar(rden[:, k:k + 1], ps[:, b, MLV:MLV + 1], -1.0, None, ALU.mult))
                        link(dve.scalar_tensor_tensor(out=den[:, k:k + 1], in0=ps[:, b, MLV:MLV + 1],
                                                      scalar=cols_a[:, 1, t, g:g + 1], in1=rden[:, k:k + 1],
                                                      op0=ALU.max, op1=ALU.max))
                        link(dve.reciprocal(rden[:, k:k + 1], den[:, k:k + 1]))
                        dve.tensor_scalar(xn[:, t, g * MLV:(g + 1) * MLV], ps[:, b, 0:MLV], rden[:, k:k + 1], None,
                                          ALU.mult).then_inc(hrow_ok, 1)
            lo_upto(C_MLOUT + 2)
            dve.wait_ge(nhi_ok, 2)
            dve.tensor_tensor(narrow_lo[:, :, :], router_w[:, :, :], narrow_hi[:, :, :].bitcast(F32),
                              ALU.subtract).then_inc(nlo_ok, 1)
            dve.wait_ge(hroot_ok, 1)
            link(dve.reciprocal(head_rs[:, :], head_root[:, :]))
            dve.wait_ge(osig_ok, 2)
            for t in range(TT):
                for g in range(MLH):
                    v = xn[:, t, g * MLV:(g + 1) * MLV]
                    ins = dve.scalar_tensor_tensor(out=v, in0=v, scalar=head_rs[:, 2 * g + t:2 * g + t + 1],
                                                   in1=osig[:, t, g * MLV:(g + 1) * MLV], op0=ALU.mult, op1=ALU.mult)
                ins.then_inc(hg_ok, 1)
            norm_split(12, V_MH)
            lo_upto(C_EXP)
            for n in range(2):
                for i in range(TT):
                    dve.wait_ge(used, C_MLOUT + 2 * n + 2)
                    add_h(4 + 2 * n + i, i, n)
            lo_upto(C_EXP + 2)
            norm(3)
            norm_split(16, V_FFNO)
            dve.wait_ge(nrow_mm, 2)
            dve.tensor_copy(narrow_row, ps[0:8, 7, T:2 * T]).then_inc(nrow_ok, 1)
            dve.wait_ge(r_mm, 1)
            link(dve.tensor_copy(logit[:, :, :], ps[:, 7, 0:16].rearrange("p (i e) -> p i e", i=TT)))
            for i in range(TT):
                link(dve.max(top8[:, i, :], logit[:, i, :]))
                link(dve.max_index(top8_i[:, i, :], top8[:, i, :], logit[:, i, :]))
            link(dve.tensor_copy(top2_f[:, :, :], top8_i[:, :, 0:2]))
            dve.tensor_scalar(ntop[:, :].unsqueeze(2), top8[:, :, 0:1], -1.0, None, ALU.mult).then_inc(r_d, 1)
            lo_upto(C_EXP + 3)
            dve.wait_ge(r_a, 1)
            link(dve.tensor_scalar(pair_d[:, :], pair_e[:, :], 1.0, None, ALU.add))
            link(dve.reciprocal(pair_w1[:, :], pair_d[:, :]))
            link(dve.tensor_tensor(pair_w2[:, :], pair_e[:, :], pair_w1[:, :], ALU.mult))
            for i in range(TT):
                dve.tensor_scalar(chosen1[:, i, :], slot_no[:, 0:8], top2_f[:, i, 0:1], None, ALU.is_equal)
                link(dve.tensor_scalar(chosen2[:, i, :], slot_no[:, 0:8], top2_f[:, i, 1:2], None, ALU.is_equal))
                link(dve.tensor_scalar(share1[:, i, :], chosen1[:, i, :], pair_w1[:, i:i + 1], None, ALU.mult))
                link(dve.scalar_tensor_tensor(out=share[:, i, 0:8], in0=chosen2[:, i, :], scalar=pair_w2[:, i:i + 1],
                                              in1=share1[:, i, :], op0=ALU.mult, op1=ALU.add))
            dve.tensor_tensor(chosen[:, :, :], chosen1[:, :, :], chosen2[:, :, :], ALU.add).then_inc(r_d, 1)
            dve.wait_ge(rank_mm, 1)
            link(dve.memset(slot_of[:, :, 8:9], FAR))
            for i in range(TT):
                link(dve.scalar_tensor_tensor(out=slot_of[:, i, 0:8], in0=chosen[:, i, :], scalar=-FAR,
                                              in1=ps[:, 7, 16 + 8 * i:24 + 8 * i], op0=ALU.mult, op1=ALU.add))
            link(dve.tensor_scalar(slot_of[:, :, 0:8], slot_of[:, :, 0:8], FAR, None, ALU.add))
            link(dve.tensor_scalar(slot_of2[:, :, :], slot_of[:, :, :], -float(P), None, ALU.add))
            link(dve.tensor_scalar(over[:, :], ps[:, 7, 32:40], float(P), None, ALU.is_gt))
            link(dve.tensor_scalar(over_key[:, :], slot_no[:, 0:8], -1.0, 8.0, ALU.mult, ALU.add))
            link(dve.tensor_tensor(over_key[:, :], over_key[:, :], over[:, :], ALU.mult))
            link(dve.max(over_top[:, :], over_key[:, :]))
            link(dve.tensor_reduce(over_tab[:, 3:4], over[:, :], AX.X, ALU.add))
            link(dve.tensor_scalar(over_tab[:, 0:3], over_top[:, 0:3], -1.0, 8.0, ALU.mult, ALU.add))
            link(dve.tensor_scalar(over_tab[:, 0:3], over_tab[:, 0:3], 7.0, None, ALU.min))
            dve.tensor_copy(over_i[:, :], over_tab[:, :]).then_inc(table_ok, 1)

            def make_pick(table, e):
                for i in range(TT):
                    ins = dve.tensor_scalar(pick[:, i, :], slot_no[:, :], table[:, i, bass.ds(e, 1)], None, ALU.is_equal)
                ins.then_inc(pick_ok, 1)

            def make_pick_w(table, e):
                for i in range(TT):
                    ins = dve.tensor_scalar(pick_w[:, i, :], slot_no[:, :], table[:, i, bass.ds(e, 1)],
                                            share[:, i, bass.ds(e, 1)], ALU.is_equal, ALU.mult)
                ins.then_inc(pickw_ok, 1)

            def seg_lo(r, seg, it=0):
                dve.wait_ge(hi_made, chunk_no(r, seg, it) + 1)
                lo_at(C_EXP + r)

            def seg_gather(g, n):
                for b in range(2):
                    dve.wait_ge(gathered, n * 2 + (b + 1))
                    dve.tensor_tensor(gained[:, b, :].rearrange("p (k t) -> p k t", t=P),
                                      ps[:, 5 + b, :].rearrange("p (k t) -> p k t", t=P),
                                      vec_t[:, V_FFNO + 4 * b:V_FFNO + 4 * b + 4].unsqueeze(2).to_broadcast([P, 4, P]),
                                      ALU.mult).then_inc(gain_ok, 1)
                for b in range(2):
                    dve.wait_ge(ghi_ok, g + (b + 1))
                    dve.tensor_tensor(slots_lo[:, 4 * b:4 * b + 4, :], gained[:, b, :].rearrange("p (k t) -> p k t", t=P),
                                      slots_hi[:, 4 * b:4 * b + 4, :].bitcast(F32), ALU.subtract).then_inc(glo_ok, 1)

            def seg_hidden(blk):
                dve.wait_ge(e_silu, blk + 1)
                dve.tensor_tensor(h_row, g_act, ps[:, 1, :], ALU.mult).then_inc(e_h, 1)

            def seg_hidden_lo(blk):
                dve.wait_ge(e_hi, blk + 1)
                dve.tensor_tensor(exp_lo, ps[:, 2, :].rearrange("p (m t) -> p m t", m=4), exp_hi.bitcast(F32),
                                  ALU.subtract).then_inc(e_lo, 1)

            def segment(seg, main, expert, table):
                make_pick_w(table, expert)
                if main:
                    make_pick(table, expert + 1)
                seg_lo(3, seg)
                seg_lo(FIRST, seg)
                if main:
                    with dve.If(seg > 0):
                        add_back(seg)
                seg_lo(FIRST + 1, seg)
                seg_hidden(seg * NEB)
                with dve.Fori(0, NEB - 1) as it:
                    blk = seg * NEB + it
                    seg_lo(FIRST + 2, seg, it)
                    seg_lo(FIRST + 3, seg, it)
                    seg_hidden_lo(blk)
                    seg_lo(FIRST + 4, seg, it)
                    seg_lo(FIRST + 5, seg, it)
                    seg_hidden(blk + 1)
                    seg_lo(FIRST + 6, seg, it)
                    seg_lo(FIRST + 7, seg, it)
                seg_hidden_lo(seg * NEB + (NEB - 1))
                if main:
                    with dve.If(seg < NE - 1):
                        seg_lo(PER_EXP, seg)
                    seg_gather(seg * 2 + (G_EXP + 2), seg + 1)
                    with dve.If(seg < NE - 1):
                        seg_lo(PER_EXP + 1, seg)
                        seg_lo(PER_EXP + 2, seg)

            def add_back(n):
                dve.wait_ge(comb_add, n * 4 + 1)
                for q, bank in enumerate((5, 6, 7, 2)):
                    i, m = q // 2, q % 2
                    dve.wait_ge(comb_mm, n * 4 + (q + 1))
                    v = h[:, i, 512 * m:512 * m + 512]
                    dve.tensor_tensor(v, v, ps[:, bank, :], ALU.add).then_inc(comb_add, 1)

            dve.wait_ge(dve_step, steps[0])
            make_pick(slot_of, 0)
            seg_gather(G_EXP, 0)
            with dve.Fori(0, NE) as e:
                segment(e, True, e, slot_of)
            add_back(NE)
            n_over = dve.value_load(over_i[0:1, 3:4], min_val=0, max_val=3)
            with dve.Fori(0, 3) as j:
                with dve.If(n_over > j):
                    expert = dve.value_load(over_i[0:1, bass.ds(j, 1)], min_val=0, max_val=NE - 1)
                    make_pick(slot_of2, expert)
                    seg_lo(0, j + NE)
                    seg_gather(j * 2 + (G_EXP + 2 * (NE + 1)), j + (NE + 1))
                    seg_lo(1, j + NE)
                    seg_lo(2, j + NE)
                    segment(j + NE, False, expert, slot_of2)
                    add_back(j + (NE + 1))
            dve.drain()
            dve.tensor_copy(share1[:, 0, 0:1], h[:, 0, 0:1]).then_inc(h_ok, 1)
            dve.wait_ge(final_in, 16)
            dve.wait_ge(rooted, 5)
            link(dve.reciprocal(rstd[:, 4, :], root[:, 4, :]))
            for i in range(TT):
                dve.scalar_tensor_tensor(out=xn[:, i, :], in0=h[:, i, :], scalar=rstd[:, 4, i:i + 1],
                                         in1=final_g, op0=ALU.mult, op1=ALU.mult).then_inc(fin_ok, 1)

        @block.tensor
        def _(pe):
            def x_still(out, hi_l, lo_l, wh, wl, start, stop):
                pe.matmul(out, hi_l, wl, start=start, stop=False, skip_group_check=True)
                pe.matmul(out, hi_l, wh, start=False, stop=False, skip_group_check=True)
                return pe.matmul(out, lo_l, wh, start=False, stop=stop, skip_group_check=True)

            def w_still(out, wh, wl, xh, xl, start, stop):
                pe.matmul(out, wl, xh, start=start, stop=False, skip_group_check=True)
                pe.matmul(out, wh, xl, start=False, stop=False, skip_group_check=True)
                return pe.matmul(out, wh, xh, start=False, stop=stop, skip_group_check=True)

            def halves(c, a):
                s = split_slot(c)
                return (w_hi[:, s, :].rearrange("p (a n) -> p a n", a=a), w_lo[:, s, :].rearrange("p (a n) -> p a n", a=a))

            def turn_rows(n_ready, sem_ready, banks=(0, 1, 2, 3)):
                for i in range(TT):
                    pe.wait_ge(sem_ready, n_ready + i + 1)
                    for k in range(KT):
                        ins = pe.transpose(ps[:, banks[2 * i + k // 4], (k % 4) * P:(k % 4 + 1) * P],
                                           xn[:, i, k * P:(k + 1) * P], ident[:, :])
                        if k % 4 == 3:
                            ins.then_inc(turned, 1)

            pe.wait_ge(consts, 1)
            pe.wait_ge(vec_in, 7 * 16)
            pe.transpose(ps[:, 7, 0:NVEC], vecs[:, :], ident[0:NVEC, 0:NVEC]).then_inc(vec_tr, 1)
            turn_rows(0, xn_ok)

            def in_proj(c0, b, turned_form):
                base = 4 * (b % 2)
                for a in range(2):
                    pe.wait_ge(lo_made, c0 + a + 1)
                    wh, wl = halves(c0 + a, 4)
                    if turned_form:
                        for m in range(4):
                            for k in range(4):
                                ins = w_still(ps[:, base + m, 0:T], wh[:, k, m * P:(m + 1) * P], wl[:, k, m * P:(m + 1) * P],
                                              xt_hi[:, 4 * a + k, :], xt_lo[:, 4 * a + k, :],
                                              a == 0 and k == 0, a == 1 and k == 3)
                    else:
                        for i in range(TT):
                            for k in range(4):
                                ins = x_still(ps[:, base + i, :], xt_hi[:, 4 * a + k, i * P:(i + 1) * P],
                                              xt_lo[:, 4 * a + k, i * P:(i + 1) * P], wh[:, k, :], wl[:, k, :],
                                              a == 0 and k == 0, a == 1 and k == 3)
                    ins.then_inc(used, 1)

            def out_proj(c0, base):
                for n in range(2):
                    for a in range(2):
                        c = c0 + 2 * n + a
                        pe.wait_ge(lo_made, c + 1)
                        wh, wl = halves(c, 4)
                        for i in range(TT):
                            for k in range(4):
                                ins = x_still(ps[:, base + 2 * n + i, :], xt_hi[:, 4 * a + k, i * P:(i + 1) * P],
                                              xt_lo[:, 4 * a + k, i * P:(i + 1) * P], wh[:, k, :], wl[:, k, :],
                                              a == 0 and k == 0, a == 1 and k == 3)
                        ins.then_inc(used, 1)

            pe.wait_ge(glo_ok, 4)
            for b in range(6):
                if b >= 2:
                    s, n = {2: (q_out, 1), 3: (kv_out, 1), 4: (kv_out, 2), 5: (q_out, 2)}[b]
                    pe.wait_ge(s, n)
                in_proj(2 * b, b, b in (0, 1, 3, 4))

            pe.wait_ge(kv_out, 4)
            for i in range(2 * NPAIR + 2):
                if i < 2 * NPAIR:
                    u, z = i // 2, 2 * (i % 2)
                    if i % 2 == 0:
                        if u:
                            pe.wait_ge(wexp_ok, u)
                        for a in range(2):
                            r = slice(HD * a, HD * a + HD)
                            pe.matmul(ps[:, z + a, 0:T], qk[r, 4 + u, 0:P], qk[r, u, 0:T],
                                      start=True, stop=False, skip_group_check=True)
                            ins = pe.matmul(ps[:, z + a, T:384], qk[r, 4 + u, P:T], qk[r, u, P:T],
                                            start=False, stop=False, skip_group_check=True)
                    else:
                        if u:
                            pe.wait_ge(pt_ok, u)
                        for a in range(2):
                            r = slice(HD * a, HD * a + HD)
                            pe.matmul(ps[:, z + a, 0:P], qk[r, 8 + u, 0:P], qk[r, 12 + u, 0:P], start=True, stop=True)
                            ins = pe.matmul(ps[:, z + a, P:384], qk[r, 8 + u, P:T], qk[r, 12 + u, 0:T], start=True, stop=True)
                    ins.then_inc(z_done, 1)
                if 1 <= i <= 2 * NPAIR:
                    j = i - 1
                    u, z = j // 2, 2 * (j % 2)
                    if j % 2 == 0:
                        pe.wait_ge(spm_ok, u + 1)
                        for a in range(2):
                            s = work[:, u % 2, a, :]
                            pe.matmul(ps[:, z + a, 0:T], neg_tri[:, :], s[:, 0:T], start=False, stop=False, skip_group_check=True)
                            pe.matmul(ps[:, z + a, P:T], neg_one[:, :], s[:, T:384], start=False, stop=False, skip_group_check=True)
                            ins = pe.matmul(ps[:, z + a, T:384], neg_tri[:, :], s[:, T:384], start=False, stop=True,
                                            skip_group_check=True)
                    else:
                        pe.wait_ge(p_ok, u + 1)
                        for a in range(2):
                            for q in range(3):
                                ins = pe.transpose(ps[:, z + a, q * P:(q + 1) * P], work2[:, 1, a, q * P:(q + 1) * P], ident[:, :])
                    ins.then_inc(b_done, 1)
                if i >= 2:
                    j = i - 2
                    u = j // 2
                    pe.wait_ge(w_ok if j % 2 == 0 else pt_ok, u + 1)
                    if j >= 2:
                        pe.wait_ge(olo_ok, j - 1)
                    for a in range(2):
                        c = slice(HD * (2 * u + a), HD * (2 * u + a) + HD)
                        w = work2[:, 0, a, :] if j % 2 == 0 else probs_t[:, a, :]
                        o = ps[HD * a:HD * a + HD, 4 + j % 2, :]
                        pe.matmul(o[:, 0:T], v_attn[:, j % 2, 0, c], w[:, 0:T], start=True, stop=False, skip_group_check=True)
                        ins = pe.matmul(o[:, P:T], v_attn[:, j % 2, 1, c], w[:, T:384], start=False, stop=True,
                                        skip_group_check=True)
                    ins.then_inc(o_done, 1)
            pe.wait_ge(olo_ok, 2 * NPAIR)
            out_proj(C_OUT, 0)

            turn_rows(2, xn_ok)
            pe.wait_ge(glo_ok, 8)

            def d_up(n, it=0):
                if n:
                    pe.wait_ge(d_h, it * 2 + n)
                for q, c in enumerate((up_pos(n) - 1, up_pos(n))):
                    pe.wait_ge(lo_made, it * 6 + c + 1)
                    wh, wl = halves(c, KT)
                    for m in range(2):
                        for k in range(KT):
                            ins = w_still(ps[:, 2 * q + m, 0:T], wh[:, k, m * P:(m + 1) * P], wl[:, k, m * P:(m + 1) * P],
                                          xt_hi[:, k, :], xt_lo[:, k, :], k == 0, k == KT - 1)
                    ins.then_inc(used, 1)

            def d_down(n, it=0, first=False, last=False):
                c = down_pos(n)
                pe.wait_ge(lo_made, it * 6 + c + 1)
                pe.wait_ge(d_lo, it * 2 + n + 1)
                wh, wl = halves(c, 2)
                for i in range(TT):
                    for m in range(2):
                        for k in range(2):
                            ins = x_still(ps[:, 4 + 2 * i + m, :], ffn_hi[:, n % 2, k, i * P:(i + 1) * P],
                                          ffn_lo[:, n % 2, k, i * P:(i + 1) * P], wh[:, k, 512 * m:512 * m + 512],
                                          wl[:, k, 512 * m:512 * m + 512], first and k == 0, last and k == 1)
                ins.then_inc(used, 1)

            d_up(0)
            d_up(1)
            d_down(0, first=True)
            d_up(2)
            d_down(1)
            with pe.Fori(0, 4) as it:
                for n in (3, 4):
                    d_up(n, it)
                    d_down(n - 1, it)
            d_down(NFB - 1, last=True)

            turn_rows(4, xn_ok)
            pe.wait_ge(glo_ok, 12)
            pe.wait_ge(nlo_ok, 1)

            def narrow(n):
                for k in range(KT):
                    for q, (wp, xp) in enumerate(((narrow_lo, xt_lo), (narrow_hi, xt_lo), (narrow_lo, xt_hi), (narrow_hi, xt_hi))):
                        ins = pe.matmul(ps[0:8, 7, T:2 * T], wp[:, k, :], xp[:, k, :], start=(k == 0 and q == 0),
                                        stop=(k == KT - 1 and q == 3))
                ins.then_inc(nrow_mm, 1)
                pe.wait_ge(nrow_ok, n)
                for i in range(TT):
                    ins = pe.transpose(ps[:, 7, 8 * i:8 * i + 8], narrow_row[:, i * P:(i + 1) * P], ident[0:8, 0:8])
                return ins

            narrow(1).then_inc(gate_mm, 1)
            for b in range(6):
                if b == 1:
                    pe.wait_ge(gate_d, 1)
                if b in (2, 3):
                    pe.wait_ge(mevac_a, b - 1)
                if b in (4, 5):
                    pe.wait_ge(mevac_v, b - 3)
                in_proj(C_MLIN + 2 * b, b, b < 2)
                if b == 3:
                    pe.wait_ge(gate_a, 3)
                    for i in range(TT):
                        pe.transpose(ps[0:MLH, 6, i * P:(i + 1) * P], gates[:, i, 0:4], ident[:, :])
                        ins = pe.transpose(ps[0:MLH, 6, T + i * P:T + (i + 1) * P], gates[:, i, 4:8], ident[:, :])
                    ins.then_inc(gate_pe, 1)
                if b == 4:
                    pe.wait_ge(gate_d, 4)
                    pe.wait_ge(gate_a, 4)
                    for x, src in enumerate((rows_a, rows_x)):
                        for i in range(TT):
                            ins = pe.transpose(ps[:, 6, 8 * x + 4 * i:8 * x + 4 * i + 4], src[:, i * P:(i + 1) * P],
                                               ident[0:MLH, 0:MLH])
                    ins.then_inc(gate_pe, 1)
            pe.wait_ge(qk_ok, 8)
            pe.wait_ge(osig_ok, 2)
            pe.wait_ge(dve_const, 2)
            for i in range(MLH + 1):
                if i < MLH:
                    g, b = i, 2 * (i % 2)
                    if g >= 2:
                        pe.wait_ge(pt2_ok, g - 1)
                    pe.matmul(ps[:, b, 0:T], conv_o[:, 4 + g, 0:P], conv_o[:, g, 0:T], start=True, stop=True)
                    pe.matmul(ps[:, b, T:384], conv_o[:, 4 + g, P:T], conv_o[:, g, P:T], start=True, stop=True)
                    pe.matmul(ps[:, b + 1, 0:T], head_sel[:, g, :], rows_m, start=True, stop=False, skip_group_check=True)
                    pe.matmul(ps[:, b + 1, 0:P], ident[:, :], causal[:, :], start=False, stop=True, skip_group_check=True)
                    pe.matmul(ps[:, b + 1, T:384], head_sel[:, g, :], rows_m[:, P:T], start=True, stop=False, skip_group_check=True)
                    pe.matmul(ps[:, b + 1, T:384], ident[:, :], causal[:, :], start=False, stop=True,
                              skip_group_check=True).then_inc(s_mm, 1)
                if i >= 1:
                    g = i - 1
                    b = 4 + 2 * (g % 2)
                    pe.wait_ge(pt2_ok, g + 1)
                    if g >= 2:
                        pe.wait_ge(hrow_ok, 2 * g - 2)
                    f = work2[:, g % 2, 1, :]
                    pe.matmul(ps[:, b, 0:MLV + 1], f[:, 0:P], vrow[:, 0, g, 0:MLV + 1], start=True, stop=True)
                    pe.matmul(ps[:, b + 1, 0:MLV + 1], f[:, P:T], vrow[:, 0, g, 0:MLV + 1], start=True, stop=False)
                    pe.matmul(ps[:, b + 1, 0:MLV + 1], f[:, T:384], vrow[:, 1, g, 0:MLV + 1], start=False,
                              stop=True).then_inc(num_mm, 1)
            turn_rows(0, hg_ok)
            pe.wait_ge(glo_ok, 16)
            out_proj(C_MLOUT, 4)

            turn_rows(6, xn_ok)
            pe.wait_ge(glo_ok, 20)
            pe.wait_ge(nlo_ok, 2)
            narrow(2).then_inc(r_mm, 1)
            pe.wait_ge(r_d, 2)
            pe.matmul(ps[:, 7, 16:24], before[:, :], chosen[:, 0, :], start=True, stop=True)
            pe.matmul(ps[:, 7, 24:32], ones[:, :], chosen[:, 0, :], start=True, stop=False)
            pe.matmul(ps[:, 7, 24:32], before[:, :], chosen[:, 1, :], start=False, stop=True)
            pe.matmul(ps[:, 7, 32:40], ones[:, :], chosen[:, 0, :], start=True, stop=False)
            pe.matmul(ps[:, 7, 32:40], ones[:, :], chosen[:, 1, :], start=False, stop=True).then_inc(rank_mm, 1)

            def gather(n, seg):
                pe.wait_ge(pick_ok, n + 1)
                pe.wait_ge(comb_add, seg * 4 + 5)
                for k in range(KT):
                    for i in range(TT):
                        ins = pe.matmul(ps[:, 5 + k // 4, (k % 4) * P:(k % 4 + 1) * P], xn[:, i, k * P:(k + 1) * P],
                                        pick[:, i, :], start=(i == 0), stop=(i == 1))
                    if k % 4 == 3:
                        ins.then_inc(gathered, 1)

            def up(r, bank, a, seg, it=0):
                pe.wait_ge(lo_made, chunk_no(r, seg, it) + 1)
                wh, wl = halves(C_EXP + r, 4)
                for k in range(4):
                    ins = x_still(ps[:, bank, :], slots_hi[:, 4 * a + k, :], slots_lo[:, 4 * a + k, :],
                                  wh[:, k, :], wl[:, k, :], a == 0 and k == 0, a == 1 and k == 3)
                ins.then_inc(used, 1)

            def turn_hidden(blk):
                pe.wait_ge(e_h, blk + 2)
                for m in range(4):
                    ins = pe.transpose(ps[:, 2, m * P:(m + 1) * P], h_row[:, m * P:(m + 1) * P], ident[:, :])
                ins.then_inc(e_tr, 1)

            def down(r, a, blk, seg, it=0):
                pe.wait_ge(lo_made, chunk_no(r, seg, it) + 1)
                pe.wait_ge(e_lo, blk + 1)
                wh, wl = halves(C_EXP + r, 2)
                for k in range(2):
                    for m in range(2):
                        ins = x_still(ps[:, 3 + m, :], exp_hi[:, 2 * a + k, :], exp_lo[:, 2 * a + k, :],
                                      wh[:, k, 512 * m:512 * m + 512], wl[:, k, 512 * m:512 * m + 512], False, False)
                ins.then_inc(used, 1)

            def segment(seg, main, groups):
                pe.wait_ge(glo_ok, groups)
                pe.wait_ge(e_h, seg * NEB + 1)
                up(0, 0, 0, seg)
                up(1, 0, 1, seg)
                if main:
                    with pe.If(seg > 0):
                        combine(seg, groups)
                up(2, 1, 0, seg)
                up(3, 1, 1, seg)
                pe.wait_ge(pickw_ok, seg + 1)
                pe.wait_ge(comb_add, seg * 4 + 5)
                for i in range(TT):
                    ins = pe.transpose(ps[:, 7, i * P:(i + 1) * P], pick_w[:, i, :], ident[:, :])
                ins.then_inc(pickw_tr, 1)
                for m in range(2):
                    pe.matmul(ps[:, 3 + m, :], zero_b[:, 0:P], zero_b[:, :], start=True, stop=False, skip_group_check=True)
                with pe.Fori(0, NEB - 1) as it:
                    blk = seg * NEB + it
                    pe.wait_ge(e_h, blk + 2)
                    up(FIRST, 0, 0, seg, it)
                    up(FIRST + 1, 0, 1, seg, it)
                    turn_hidden(blk)
                    up(FIRST + 2, 1, 0, seg, it)
                    up(FIRST + 3, 1, 1, seg, it)
                    down(FIRST + 4, 0, blk, seg, it)
                    down(FIRST + 5, 1, blk, seg, it)
                turn_hidden(seg * NEB + (NEB - 1))
                if main:
                    gather(seg + 1, seg)
                for a in range(2):
                    down(LAST + a, a, seg * NEB + (NEB - 1), seg)

            def combine(n, groups):
                pe.wait_ge(y_out, n + 1)
                pe.wait_ge(spread_ok, n + 1)
                pe.wait_ge(gain_ok, groups)
                for q, bank in enumerate((5, 6, 7, 2)):
                    i, m = q // 2, q % 2
                    pe.matmul(ps[:, bank, :], spread[:, i, :], y_seg[:, 512 * m:512 * m + 512],
                              start=True, stop=True).then_inc(comb_mm, 1)

            pe.wait_ge(table_ok, 1)
            gather(0, 0)
            with pe.Fori(0, NE) as e:
                segment(e, True, e * 2 + (G_EXP + 2))
            combine(NE, G_EXP + 2 * (NE + 1))
            n_over = pe.value_load(over_i[0:1, 3:4], min_val=0, max_val=3)
            with pe.Fori(0, 3) as j:
                with pe.If(n_over > j):
                    gather(j + (NE + 1), j + NE)
                    segment(j + NE, False, j * 2 + (G_EXP + 2 * (NE + 2)))
                    combine(j + (NE + 1), j * 2 + (G_EXP + 2 * (NE + 2)))


_INS = ["x", "mix_norm_even", "w_in_attn", "rel_bias", "w_out_attn", "ffn_norm_even", "w_dense_gate",
        "w_dense_up", "w_dense_down", "mix_norm_odd", "w_in_mlstm", "conv_w", "conv_b", "b_igate", "b_fgate",
        "mh_norm_g", "w_out_mlstm", "ffn_norm_odd", "w_router", "w_exp_gate", "w_exp_up", "w_exp_down",
        "final_norm_g"]


def kernel(**inputs):
    import numpy as _np
    import concourse.bacc as _bacc
    from concourse import mybir as _mybir
    from concourse.bass_utils import run_bass_kernel_spmd as _run

    nc = _bacc.Bacc("TRN2", target_bir_lowering=False, num_devices=1)
    arrays, args = {}, []
    for name in _INS:
        a = _np.ascontiguousarray(inputs[name])
        arrays[f"in_{name}_dram"] = a
        args.append(nc.dram_tensor(f"in_{name}_dram", a.shape, _mybir.dt.from_np(a.dtype), kind="ExternalInput").ap())
    args.append(nc.dram_tensor("out_dram", (1, T, D), F32, kind="ExternalOutput").ap())
    trunk(nc, *args)
    r = _run(nc, [arrays], core_ids=[0])
    return r.results[0]["out_dram"]
```
